# Optimizing a Trainium2 kernel written in Bass

```python
import math
import jax, jax.numpy as jnp
from jax import lax
import numpy as np

D_MODEL = 1024
BATCH = 1
SEQ = 512
DEPTH = 1

HEAD_DIM = 64
SB_WIDTH = D_MODEL // 2
N_HEADS_SB = SB_WIDTH // HEAD_DIM
DSA_WIDTH = D_MODEL // 2
N_HEADS_DSA = DSA_WIDTH // HEAD_DIM
KV_DIM = HEAD_DIM
IDX_HEADS = 8
IDX_DIM = 64
INDEX_TOPK_MAX = 256
BLOCK_Q = 128
REL_BUCKETS = 32
REL_MAX_DIST = 128
N_EXPERTS = 16
N_GROUPS = 4
EXPERTS_PER_GROUP = N_EXPERTS // N_GROUPS
TOP_K = 2
D_EXPERT = D_MODEL // 2
N_MOD = 6
EPS = 1e-6

IN_SIZES = [SB_WIDTH, SB_WIDTH, SB_WIDTH,
            DSA_WIDTH, KV_DIM, KV_DIM,
            IDX_HEADS * IDX_DIM, IDX_DIM, IDX_HEADS,
            D_MODEL, D_MODEL]
N_IN = int(sum(IN_SIZES))
IN_OFFSETS = [int(o) for o in np.cumsum(IN_SIZES)[:-1]]

kernel_name = "hybrid_stickbreak_dsa_grouped_moe_adaln"

def rmsnorm(x, g):
    xf = x.astype(jnp.float32)
    y = xf * lax.rsqrt(jnp.mean(xf * xf, axis=-1, keepdims=True) + EPS)
    return (y * g.astype(jnp.float32)).astype(x.dtype)

def t5_bucket(dist):
    max_exact = REL_BUCKETS // 2
    is_small = dist < max_exact
    d_f = jnp.maximum(dist, 1).astype(jnp.float32)
    large = max_exact + (jnp.log(d_f / max_exact) / math.log(REL_MAX_DIST / max_exact)
                         * (REL_BUCKETS - max_exact)).astype(jnp.int32)
    large = jnp.minimum(large, REL_BUCKETS - 1)
    return jnp.where(is_small, dist, large)

def stick_breaking_attention(q, k, v):
    B, S, H, dh = q.shape
    outs = []
    for start in range(0, S, BLOCK_Q):
        end = start + BLOCK_Q
        z = jnp.einsum('bqhd,bkhd->bhqk', q[:, start:end], k[:, :end]).astype(jnp.float32) * dh ** -0.5
        t_pos = start + jnp.arange(BLOCK_Q)[:, None]
        s_pos = jnp.arange(end)[None, :]
        before = s_pos < t_pos
        log_1m = jnp.where(before, jax.nn.log_sigmoid(-z), 0.0)
        csum = jnp.cumsum(log_1m, axis=-1)
        log_a = jax.nn.log_sigmoid(z) + (csum[..., -1:] - csum)
        a = jnp.where(before, jnp.exp(log_a), 0.0)
        outs.append(jnp.einsum('bhqk,bkhd->bqhd', a.astype(v.dtype), v[:, :end]))
    return jnp.concatenate(outs, axis=1)

def dsa_sparse_attention(q, k, v, q_idx, k_idx, w_idx, rel_bias):
    B, S, H, dh = q.shape
    ktop = min(INDEX_TOPK_MAX, S // 4)
    gather = jax.vmap(lambda arr, idx: arr[idx])
    outs = []
    for start in range(0, S, BLOCK_Q):
        end = start + BLOCK_Q
        kl = min(S, max(end, ktop))
        t_pos = start + jnp.arange(BLOCK_Q)[:, None]
        s_pos = jnp.arange(kl)[None, :]
        dots = jnp.einsum('bqhd,bkd->bqhk', q_idx[:, start:end], k_idx[:, :kl]).astype(jnp.float32)
        score = jnp.einsum('bqh,bqhk->bqk', w_idx[:, start:end].astype(jnp.float32), jax.nn.relu(dots))
        score = jnp.where(s_pos <= t_pos, score, -jnp.inf)
        _, sel = lax.top_k(score, ktop)
        k_sel = gather(k[:, :kl], sel)
        v_sel = gather(v[:, :kl], sel)
        dist = t_pos[None] - sel
        valid = dist >= 0
        bias = rel_bias[t5_bucket(jnp.maximum(dist, 0))]
        logits = (jnp.einsum('bqhd,bqkd->bhqk', q[:, start:end], k_sel).astype(jnp.float32) * dh ** -0.5
                  + jnp.transpose(bias, (0, 3, 1, 2)).astype(jnp.float32))
        logits = jnp.where(valid[:, None], logits, -jnp.inf)
        p = jax.nn.softmax(logits, axis=-1)
        outs.append(jnp.einsum('bhqk,bqkd->bqhd', p.astype(v.dtype), v_sel))
    return jnp.concatenate(outs, axis=1)

def grouped_moe(h, router_w, router_b, w_gate, w_up, w_down):
    B, S, D = h.shape
    t = h.reshape(-1, D)
    logits = (t @ router_w).astype(jnp.float32) + router_b.astype(jnp.float32)
    probs = jax.nn.softmax(logits, axis=-1)
    pg = probs.reshape(-1, N_GROUPS, EXPERTS_PER_GROUP)
    group_score = jnp.sum(lax.top_k(pg, TOP_K)[0], axis=-1)
    g = jnp.argmax(group_score, axis=-1)
    in_group = jnp.take_along_axis(pg, g[:, None, None], axis=1)[:, 0]
    vals, local = lax.top_k(in_group, TOP_K)
    experts = g[:, None] * EXPERTS_PER_GROUP + local
    weights = vals / jnp.sum(vals, axis=-1, keepdims=True)
    combine = jnp.sum(jax.nn.one_hot(experts, N_EXPERTS, dtype=jnp.float32) * weights[..., None], axis=1)
    hidden = jax.nn.silu(jnp.einsum('td,edf->tef', t, w_gate)) * jnp.einsum('td,edf->tef', t, w_up)
    hidden = hidden * combine[:, :, None].astype(hidden.dtype)
    y = jnp.einsum('tef,efd->td', hidden, w_down)
    return y.reshape(B, S, D)

def setup_inputs(seed: int = 0) -> dict:
    key = jax.random.key(seed)
    ks = jax.random.split(key, 20)
    f32 = jnp.float32
    nrm = lambda k, shape, s: jax.random.normal(k, shape, f32) * s
    return {
        "x": nrm(ks[0], (BATCH, SEQ, D_MODEL), 1.0),
        "c": nrm(ks[1], (BATCH, D_MODEL), 1.0),
        "w_ada": nrm(ks[2], (DEPTH, D_MODEL, N_MOD * D_MODEL), 0.5 * D_MODEL ** -0.5),
        "b_ada": nrm(ks[3], (DEPTH, N_MOD * D_MODEL), 0.02),
        "norm1_g": 1.0 + nrm(ks[4], (DEPTH, D_MODEL), 0.02),
        "w_in": nrm(ks[5], (DEPTH, D_MODEL, N_IN), D_MODEL ** -0.5),
        "q_norm_g": 1.0 + nrm(ks[6], (DEPTH, HEAD_DIM), 0.02),
        "k_norm_g": 1.0 + nrm(ks[7], (DEPTH, KV_DIM), 0.02),
        "rel_bias": nrm(ks[8], (REL_BUCKETS, N_HEADS_DSA), 0.5),
        "w_o_a": nrm(ks[9], (DEPTH, SB_WIDTH, D_MODEL), SB_WIDTH ** -0.5),
        "w_o_b": nrm(ks[10], (DEPTH, DSA_WIDTH, D_MODEL), DSA_WIDTH ** -0.5),
        "w_out": nrm(ks[11], (DEPTH, D_MODEL, D_MODEL), D_MODEL ** -0.5),
        "norm2_g": 1.0 + nrm(ks[12], (DEPTH, D_MODEL), 0.02),
        "router_w": nrm(ks[13], (D_MODEL, N_EXPERTS), D_MODEL ** -0.5),
        "router_b": nrm(ks[14], (N_EXPERTS,), 0.01),
        "w_gate": nrm(ks[15], (DEPTH, N_EXPERTS, D_MODEL, D_EXPERT), D_MODEL ** -0.5),
        "w_up": nrm(ks[16], (DEPTH, N_EXPERTS, D_MODEL, D_EXPERT), D_MODEL ** -0.5),
        "w_down": nrm(ks[17], (DEPTH, N_EXPERTS, D_EXPERT, D_MODEL), D_EXPERT ** -0.5),
    }

def reference(x, c, w_ada, b_ada, norm1_g, w_in, q_norm_g, k_norm_g, rel_bias,
              w_o_a, w_o_b, w_out, norm2_g, router_w, router_b, w_gate, w_up, w_down):
    B, S, D = x.shape
    for l in range(DEPTH):
        mod = jax.nn.silu(c) @ w_ada[l] + b_ada[l]
        shift1, scale1, gate1, shift2, scale2, gate2 = [m[:, None, :] for m in jnp.split(mod, N_MOD, axis=-1)]

        h = rmsnorm(x, norm1_g[l]) * (1.0 + scale1) + shift1
        proj = h @ w_in[l]
        (q_a, k_a, v_a, q_b, k_b, v_b, q_i, k_i, w_i, g_a, g_b) = jnp.split(proj, IN_OFFSETS, axis=-1)

        q_a = q_a.reshape(B, S, N_HEADS_SB, HEAD_DIM)
        k_a = k_a.reshape(B, S, N_HEADS_SB, HEAD_DIM)
        v_a = v_a.reshape(B, S, N_HEADS_SB, HEAD_DIM)
        o_a = stick_breaking_attention(q_a, k_a, v_a).reshape(B, S, SB_WIDTH)

        q_b = rmsnorm(q_b.reshape(B, S, N_HEADS_DSA, HEAD_DIM), q_norm_g[l])
        k_b = rmsnorm(k_b, k_norm_g[l])
        q_i = q_i.reshape(B, S, IDX_HEADS, IDX_DIM)
        o_b = dsa_sparse_attention(q_b, k_b, v_b, q_i, k_i, w_i, rel_bias).reshape(B, S, DSA_WIDTH)

        merged = jax.nn.sigmoid(g_a) * (o_a @ w_o_a[l]) + jax.nn.sigmoid(g_b) * (o_b @ w_o_b[l])
        x = x + gate1 * (merged @ w_out[l])

        h2 = rmsnorm(x, norm2_g[l]) * (1.0 + scale2) + shift2
        x = x + gate2 * grouped_moe(h2, router_w, router_b, w_gate[l], w_up[l], w_down[l])
    return x


_drawn_inputs = setup_inputs


def setup_inputs(seed=0):
    import zlib

    import numpy as np

    out = dict(_drawn_inputs(seed))
    spreads = {}
    factors = {'norm1_g': 5.329,
     'q_norm_g': 8.0,
     'k_norm_g': 8.0,
     'rel_bias': 3.441,
     'norm2_g': 3.106,
     'router_b': 3.045}
    for name, (base, spread) in spreads.items():
        noise = np.random.default_rng([zlib.crc32(name.encode()), seed]).standard_normal(out[name].shape)
        drawn = base * np.exp(spread * noise) if base else spread * noise
        out[name] = __import__('jax').numpy.asarray(drawn.astype(out[name].dtype))
    for name, factor in factors.items():
        out[name] = (out[name] * factor).astype(out[name].dtype)
    return out
```

```python
from contextlib import ExitStack

import numpy as np

import concourse.bass as bass
from concourse import mybir

F32 = mybir.dt.float32
F32R = mybir.dt.float32r
BF16 = mybir.dt.bfloat16
I32 = mybir.dt.int32
ALU = mybir.AluOpType
ACT = mybir.ActivationFunctionType
AX = mybir.AxisListType

P = 128
D = 1024
S = 512
KD = D // P
NT = S // P
DH = 64
HEADS = 8
HW = HEADS * DH
TOPK = min(256, S // 4)
N_EXP = 16
GROUPS = 4
EPG = N_EXP // GROUPS
F_EXP = D // 2
EPS = 1e-6
BUCKETS = 32
BUCKET_DIST = 128
BIAS_LEN = 640
SCALE = DH ** -0.5
BIG_NEG = -1.0e30
FUTURE = -3.0e38
TAKEN = -2.0e38
PASSES = S // P

C_QA, C_KA, C_VA, C_QB = 0, HW, 2 * HW, 3 * HW
C_KVB = 4 * HW
C_QI = C_KVB + 2 * DH
C_KI = C_QI + HW
C_WI = C_KI + DH
C_GA = C_WI + HEADS
C_GB = C_GA + D

RAW = 4
SPL = 3
CH = 2048
EC = 6
E_RAW = 3
E_SPL = 4


def bucket_onehot():
    dist = np.maximum(S - 1 - np.arange(BIAS_LEN), 0)
    exact = BUCKETS // 2
    f = np.maximum(dist, 1).astype(np.float32)
    large = exact + (np.log(f / np.float32(exact)) / np.float32(np.log(BUCKET_DIST / exact))
                     * np.float32(BUCKETS - exact)).astype(np.int32)
    b = np.where(dist < exact, dist, np.minimum(large, BUCKETS - 1))
    return (np.arange(BUCKETS)[:, None] == b[None, :]).astype(np.float32)


def hybrid_layer(nc, x, c, w_ada, b_ada, norm1_g, w_in, q_norm_g, k_norm_g, rel_bias, w_o_a, w_o_b,
                 w_out, norm2_g, router_w, router_b, w_gate, w_up, w_down, onehot, out):
    mod_d = nc.dram_tensor("mod_scratch", [2, 1, 2 * D], F32, kind="Internal").ap()
    bias_d = nc.dram_tensor("bias_scratch", [HEADS, BIAS_LEN], F32, kind="Internal").ap()

    toep_d = nc.dram_tensor("toeplitz_scratch", [P, HEADS, S], F32, kind="Internal").ap()

    BASE = 16640

    def at(name, shape, dt, kb):
        assert BASE + kb * 1024 + int(np.prod(shape[1:])) * (2 if dt == BF16 else 4) <= 229368
        return nc.alloc_sbuf_tensor_at(name, [P] + shape, dt, offset=BASE + int(kb * 1024))

    raw = [at(f"raw{i}", [CH], F32, 8 * i) for i in range(RAW)]
    w_hi = [at(f"w_hi{i}", [CH], F32R, 32 + 16 * i) for i in range(SPL)]
    w_lo = [at(f"w_lo{i}", [CH], F32R, 40 + 16 * i) for i in range(SPL)]
    act_hi = at("act_hi", [KD, S], F32R, 80)
    act_lo = at("act_lo", [KD, S], F32R, 96)
    h2_hi = act_hi[:, :, :].rearrange("p k s -> p (k s)").rearrange("p (t d) -> p t d", t=NT)
    h2_lo = act_lo[:, :, :].rearrange("p k s -> p (k s)").rearrange("p (t d) -> p t d", t=NT)
    xres = at("xres", [NT, D], F32, 112)
    qkn = at("qkn", [NT, 10, DH], F32, 112)
    masks = at("masks", [NT, S], BF16, 112)
    toep = [at("toepA", [4, S], F32, 116), at("toepB", [4, S], F32, 174)]
    score = [at(f"score{i}", [S], F32, 124 + 2 * i) for i in range(2)]
    qaT = at("qaT", [4, S], F32, 128)
    kaT = at("kaT", [4, S], F32, 136)
    qiT = at("qiT", [4, S], F32, 144)
    qbT = at("qbT", [4, S], F32, 152)
    oaT = [at("oaT_hi", [4, S], F32R, 128), at("oaT_lo", [4, S], F32R, 136)]
    obT = [at("obT_hi", [4, S], F32R, 152), at("obT_lo", [4, S], F32R, 144)]
    va = at("va", [NT, HW], F32, 160)
    kiT = at("kiT", [S], F32, 168)
    kbT = at("kbT", [S], F32, 170)
    vb = at("vb", [NT, P], F32, 172)
    oh_sb = at("oh_sb", [BIAS_LEN], F32, 128)
    rel_sb = at("rel_sb", [HEADS], F32, 131)
    bv_sb = at("bv_sb", [BIAS_LEN], F32, 132)
    toep_r = at("toep_r", [HEADS, S], F32, 136)
    toep_f = at("toep_f", [HEADS, S], F32, 152)
    flip = at("flip", [P], F32, 168)
    acc = at("acc", [2 * D], F32, 174)
    hn = [at(f"hn{i}", [D], F32, 182 + 4 * i) for i in range(2)]
    modrow = at("modrow", [2 * D], F32, 190)
    shift1 = at("shift1", [D], F32, 190)
    amp1 = at("amp1", [D], F32, 194)
    g1row = at("g1row", [D], F32, 198)
    qk_sq = at("qk_sq", [NT, 10, DH], F32, 174)
    sp_len = sum(S - P * i for i in range(NT))
    spb = [at(f"sp{i}", [sp_len], F32, 174 + 5 * i) for i in range(2)]
    ab = [at(f"ab{i}", [sp_len], F32, 184 + 5 * i) for i in range(2)]
    sig = [at(f"sig_tmp{i}", [S], F32, 194 + 2 * i) for i in range(2)]
    rel = [at(f"relu_tmp{i}", [S], F32, 198 + 2 * i) for i in range(2)]
    lrow = [at(f"lrow{i}", [S], F32, 182 + 2 * i) for i in range(4)]
    pT = [at("pT0", [NT, S], F32, 190), at("pT1", [NT, S], F32, 160)]
    gsig = [at("gsig0", [4, S], F32, 174), at("gsig1", [4, S], F32, 160)]
    merged = at("merged", [KD, S], F32, 182)
    etmp = [at(f"etmp{i}", [S], F32, 198 + 2 * i) for i in range(2)]
    gate1 = at("gate1", [D], F32, 168)
    junk = at("junk", [D], F32, 128)
    h2f = [at(f"h2f{i}", [D], F32, (160, 164, 174, 178)[i]) for i in range(NT)]
    shift2 = at("shift2", [D], F32, 144)
    amp2 = at("amp2", [D], F32, 148)
    g2row = at("g2row", [D], F32, 152)
    h2T = at("h2T", [KD, S], F32, 182)
    NG = NT * GROUPS
    r_gt = at("r_gt", [NG, EPG, EPG], F32, 132)
    r_ge = at("r_ge", [NG, EPG, EPG], F32, 133)
    r_top = at("r_top", [NG, EPG], F32, 134)
    r_pr = at("r_pr", [NG, EPG], F32, 134.5)
    r_gs = at("r_gs", [NT, GROUPS], F32, 135)
    r_best = at("r_best", [NT, GROUPS], F32, 135.25)
    r_tot = at("r_tot", [NT], F32, 135.5)
    yacc = at("yacc", [NT, D], F32, 128)
    hgT_hi = at("hgT_hi", [2, KD, P], F32R, 144)
    hgT_lo = at("hgT_lo", [2, KD, P], F32R, 152)
    ye_hi = [at("ye_hi0", [D], F32R, 160), at("ye_hi1", [D], F32R, 186)]
    ye_lo = [at("ye_lo0", [D], F32R, 164), at("ye_lo1", [D], F32R, 190)]
    sel = at("sel", [NT, 2, P], F32R, 168)
    silu = at("silu", [F_EXP], F32, 172)
    selT = [at(f"selT{i}", [NT, P], F32R, 174 + 2 * i) for i in range(2)]
    hid = at("hid", [F_EXP], F32, 178)
    hidT_hi = at("hidT_hi", [4, P], F32R, 180)
    hidT_lo = at("hidT_lo", [4, P], F32R, 182)
    gate2 = at("gate2", [D], F32, 186)
    posm = at("posm", [NT, N_EXP], F32, 184)
    comb = at("comb", [NT, N_EXP], F32, 184.5)
    slot_w = at("slot_w", [2], F32, 185)
    e_hi = w_hi + [at("w_hi3", [CH], F32R, 24)]
    e_lo = w_lo + [at("w_lo3", [CH], F32R, 194)]
    small = [202.0]

    def tiny(name, shape, dt=F32):
        kb = small[0]
        n = int(np.prod(shape)) * (2 if dt == BF16 else 4)
        small[0] = kb + (n + 31) // 32 * 32 / 1024
        return at(name, shape, dt, kb)

    ident = tiny("ident", [P])
    ones = tiny("ones", [P])
    negones = tiny("negones", [P])
    negtri = tiny("negtri", [P])
    before = tiny("before", [P])
    identb = tiny("identb", [P], BF16)
    neg_ge = tiny("neg_ge", [P], BF16)
    neg_gt = tiny("neg_gt", [P], BF16)
    iota = tiny("iota", [P])
    c_col = tiny("c_col", [KD])
    sc_col = tiny("sc_col", [KD])
    qkg = tiny("qkg", [2 * DH])
    rw = tiny("rw", [KD, N_EXP])
    rb = tiny("rb", [N_EXP])
    epsc = tiny("epsc", [1])
    wi = tiny("wi", [NT, HEADS])
    st = tiny("st", [NT, 10])
    m8 = [tiny(f"m8_{i}", [8]) for i in range(2)]
    nmax = tiny("nmax", [4])
    rsum = tiny("rsum", [4])
    over_f = tiny("over_f", [1])
    over = tiny("over", [1], I32)

    with ExitStack() as ctx:
        ps = [ctx.enter_context(nc.psum_tensor(f"ps{i}", [P, 512], F32)) for i in range(8)]

        def sem(name):
            return ctx.enter_context(nc.semaphore(name))

        wk = w_in[0].rearrange("(c k p) n -> c p k n", k=4, p=P)

        def cols(buf, n0, n1, nk=4):
            return buf[:, :].rearrange("p (k n) -> p k n", k=nk)[:, :, n0:n1]

        chunks = []

        def add_w(name, pieces, nk=4):
            chunks.append((name, nk, pieces))

        def add_in(name, col):
            for h in range(2):
                add_w(name, [(0, 512, wk[h][:, :, col:col + 512])])

        ada = w_ada[0].rearrange("(k p) n -> k p n", p=P)
        ada_list = [(f"ada{part}", 1, [(0, 2 * D, ada[k][:, part * 2 * D:(part + 1) * 2 * D].unsqueeze(1))])
                    for part in range(3) for k in range(KD)]
        chunks += ada_list[:KD]
        add_in("qa", C_QA)
        add_in("ka", C_KA)
        add_in("va", C_VA)
        add_in("qi", C_QI)
        for h in range(2):
            add_w("misc", [(0, 2 * DH, wk[h][:, :, C_KVB:C_KVB + 2 * DH]),
                           (2 * DH, 3 * DH, wk[h][:, :, C_KI:C_KI + DH]),
                           (3 * DH, 4 * DH + HEADS, wk[h][:, :, C_KI:C_KI + DH + HEADS])])
        add_in("qb", C_QB)
        mixed, rest = chunks[:KD], ada_list[KD:]
        for n, ch in enumerate(chunks[KD:]):
            mixed.append(ch)
            if rest:
                mixed.append(rest.pop(0))
        chunks = mixed + rest
        oak = w_o_a[0].rearrange("(k p) n -> p k n", p=P)
        obk = w_o_b[0].rearrange("(k p) n -> p k n", p=P)
        for half in range(2):
            add_in(f"ga{half}", C_GA + 512 * half)
            add_w(f"oa{half}", [(0, 512, oak[:, :, 512 * half:512 * half + 512])])
            add_in(f"gb{half}", C_GB + 512 * half)
            add_w(f"ob{half}", [(0, 512, obk[:, :, 512 * half:512 * half + 512])])
        wo = w_out[0].rearrange("(c k p) n -> c p k n", k=4, p=P)
        for half in range(2):
            for h in range(2):
                add_w(f"wo{half}", [(0, 512, wo[h][:, :, 512 * half:512 * half + 512])])
        N_RAW = len(chunks)
        assert N_RAW % RAW == 0
        first = {}
        for n, ch in enumerate(chunks):
            first.setdefault(ch[0], []).append(n)
        w_of = {}
        for n, ch in enumerate(chunks):
            if not ch[0].startswith("ada"):
                w_of[n] = len(w_of)
        N_W = len(w_of)
        slot_count, fill = [0] * RAW, []
        for n, ch in enumerate(chunks):
            slot_count[n % RAW] += 16 * len(ch[2])
            fill.append(slot_count[n % RAW])

        raw_in = [sem(f"raw_in{i}") for i in range(RAW)]
        chunk_split = sem("chunk_split")
        hi_ready = sem("hi_ready")
        w_used = sem("w_used")
        ld_x, ld_c, ld_rows, ld_small, ld_rel = (sem(n) for n in ("ld_x", "ld_c", "ld_rows", "ld_small", "ld_rel"))
        ld_toepA, ld_toepB, ld_x2, ld_g1, ld_r2, ld_g2 = (
            sem(n) for n in ("ld_toepA", "ld_toepB", "ld_x2", "ld_gate1", "ld_rows2", "ld_gate2"))
        ld_bada = sem("ld_bada")
        ld_toepR, toep_ps, toep_sb, st_toep = sem("ld_toepR"), sem("toep_ps"), sem("toep_sb"), sem("st_toep")
        st_bias, st_mod, st_out = sem("st_bias"), sem("st_mod"), sem("st_out")
        const_ready = sem("const_ready")
        pool_chain = sem("pool_chain")
        dve_chain = sem("dve_chain")
        act_chain = sem("act_chain")
        sc_ready = sem("sc_ready")
        bias_ps, bias_sb = sem("bias_ps"), sem("bias_sb")
        seg_ready = sem("seg_ready")
        evac = [sem("evac_low"), sem("evac_high")]
        h_ss, h_rs, h_rows, hT_ps, hT_hi, hT_sp = (sem(n) for n in ("h_ss", "h_rs", "h_rows", "hT_ps", "hT_hi", "hT_sp"))
        qk_var, qk_sd, qk_norm = sem("qk_var"), sem("qk_sd"), sem("qk_norm")
        z_ps, z_soft, sp_ready, s_ps, a_ready = (
            sem(n) for n in ("z_ps", "z_soft", "sp_ready", "s_ps", "a_ready"))
        oa_ps, oa_hi, oa_sp = sem("oa_ps"), sem("oa_hi"), sem("oa_sp")
        side_ps, side_sb = sem("side_ps"), sem("side_sb")
        score_ok, score_cut = sem("score_ok"), sem("score_cut")
        mask_ready = sem("mask_ready")
        l_ps, l_sb, p_exp, p_norm, pT_ps, pT_sb = (
            sem(n) for n in ("l_ps", "l_sb", "p_exp", "p_norm", "pT_ps", "pT_sb"))
        ob_ps, ob_hi, ob_sp = sem("ob_ps"), sem("ob_hi"), sem("ob_sp")
        merged_ok, m_hi, m_sp = sem("merged_ok"), sem("m_hi"), sem("m_sp")
        x1_ready, h2_ss, h2_sd, h2_rows, h2_hiR, h2_sp = (
            sem(n) for n in ("x1_ready", "h2_ss", "h2_sd", "h2_rows", "h2_hi_ready", "h2_split"))
        h2T_ps, h2T_sb, r_ps, r_exp, r_sel, pos_ps, route_ok = (
            sem(n) for n in ("h2T_ps", "h2T_sb", "router_ps", "router_exp", "route_sel", "pos_ps", "route_ok"))
        r_lg = sem("router_logits")
        sel_ready, hg_ps, hg_hi, hg_sp, g_ps, u_ps, silu_ok, hid_ok, hidT_ps, hidT_h, hidT_sp = (
            sem(n) for n in ("sel_ready", "hg_ps", "hg_hi", "hg_split", "gate_ps", "up_ps", "silu_ok", "hid_ok",
                             "hidT_ps", "hidT_hi", "hidT_split"))
        y_ps, y_hi, y_sp, selT_ps, selT_sb, sc_ps, yadd = (
            sem(n) for n in ("y_ps", "y_hi", "y_split", "selT_ps", "selT_sb", "scatter_ps", "yadd"))
        posm_ok = sem("posm_ok")
        ws_ps, ws_sb, moe_over = sem("slot_weight_ps"), sem("slot_weight_sb"), sem("moe_over")
        out_sb = sem("out_sb")

        SEGS = [("ada0", 0, None), ("qa", 0, True), ("ka", 1, True), ("va", 0, False), ("qi", 1, True),
                ("ada1", 0, None), ("misc", 1, None), ("qb", 0, False), ("ada2", 1, None)]
        for half in range(2):
            SEGS += [(f"ga{half}", 0, True), (f"oa{half}", 1, True), (f"gb{half}", 0, True), (f"ob{half}", 1, True)]
        SEGS += [("wo0", 0, False), ("wo1", 1, False)]
        seg_at = {name: n for n, (name, _, _) in enumerate(SEGS)}

        def seg_done(name, m):
            return 4 * seg_at[name] + m + 1

        def half_before(name):
            half = SEGS[seg_at[name]][1]
            return 4 * sum(1 for _, h, _ in SEGS[:seg_at[name]] if h == half)

        def bank(name, m):
            return ps[4 * SEGS[seg_at[name]][1] + m]

        used, n_used = [], 0
        for name, _, _ in SEGS:
            for n in first[name] if name[:3] != "ada" else []:
                if n == first[name][-1] or name == "misc":
                    used.append(("seg", seg_done(name, 3)))
                else:
                    n_used += 1
                    used.append(("chunk", n_used))
        N_USED = n_used

        STEPS = [(h, i) for h in range(HEADS) for i in range(NT - 1, -1, -1)]
        OFF = [sum(S - P * j for j in range(i)) for i in range(NT)]
        side = [[] for _ in STEPS]
        for i in range(1, NT):
            for h in range(HEADS):
                side[8 * (i - 1) + h].append(("idx", i, h))
        for m in range(5):
            side[8 + m].append(("tr", m, 0))
        SIDE = [t for s_ in side for t in s_]
        UNITS = [(i, h) for i in range(NT) for h in range(HEADS)]

        block = ctx.enter_context(nc.Block())

        @block.sync
        def _(sp):
            sp.dma_start(c_col[:, :], c[0].rearrange("(k p) -> p k", p=P),
                         allow_slow_non_contiguous=True).then_inc(ld_c, 16)

            def load(n):
                if n >= RAW:
                    sp.wait_ge(chunk_split, n - RAW + 1)
                name, nk, pieces = chunks[n]
                for a, b, src in pieces:
                    sp.dma_start(cols(raw[n % RAW], a, b, nk), src).then_inc(raw_in[n % RAW], 16)

            for n in range(3):
                load(n)
            sp.dma_start(xres[:, :, :], x[0].rearrange("(t p) d -> p t d", p=P)).then_inc(ld_x, 16)
            sp.dma_start(g1row[:, :], norm1_g.partition_broadcast(P).rearrange("p a d -> p (a d)")).then_inc(ld_rows, 16)
            for n in range(3, N_RAW):
                load(n)

            def expert_loads(q6, e, b):
                gv = w_gate[0].rearrange("e (c k p) f -> e c p k f", k=4, p=P)
                uv = w_up[0].rearrange("e (c k p) f -> e c p k f", k=4, p=P)
                dv = w_down[0].rearrange("e (c k p) d -> e c p k d", k=2, p=P)
                for cc in range(EC):
                    r = (EC * b + cc) % E_RAW
                    sp.wait_ge(chunk_split, q6 + (EC * b + cc) - E_RAW + 1 + N_RAW)
                    src, nk = ((gv, 4), (uv, 4), (dv, 2))[cc // 2]
                    sp.dma_start(raw[r][:, :].rearrange("p (k n) -> p k n", k=nk),
                                 src[bass.ds(e, 1), cc % 2].rearrange("a p k n -> (a p) k n")
                                 ).then_inc(raw_in[r], 16)

            with sp.Fori(0, N_EXP // 2) as q:
                for b in range(2):
                    expert_loads(q * (2 * EC), q * 2 + b, b)
            sp.wait_ge(route_ok, 1)
            more = sp.value_load(over[0:1, 0:1], min_val=0, max_val=1)
            with sp.If(more > 0):
                with sp.Fori(1, PASSES) as p:
                    with sp.Fori(0, N_EXP // 2) as q:
                        for b in range(2):
                            expert_loads(p * (N_EXP * EC) + q * (2 * EC), q * 2 + b, b)
                sp.nop()
            ov = out[0].rearrange("(t p) d -> p t d", p=P)
            for tt in range(NT):
                sp.wait_ge(out_sb, tt + 1)
                sp.dma_start(ov[:, tt], xres[:, tt]).then_inc(st_out, 16)
            sp.wait_ge(st_out, 16 * NT)

        @block.gpsimd
        def _(pool):
            n_chain = [0]

            def link(ins):
                n_chain[0] += 1
                ins.then_inc(pool_chain, 1)
                pool.wait_ge(pool_chain, n_chain[0])

            def tri(t, fill, op, base, cm, step):
                link(pool.affine_select(out=t[:, :], in_=t[:, :], compare_op=op, fill=fill, base=base,
                                        pattern=[[step, P]], channel_multiplier=cm))

            link(pool.memset(acc[:, :], 0.0))
            pool.dma_start(acc[0:1, :], b_ada[:, 0:2 * D]).then_inc(ld_bada, 16)
            pool.dma_start(oh_sb[0:BUCKETS, :], onehot).then_inc(ld_rel, 16)
            pool.dma_start(rel_sb[0:BUCKETS, :], rel_bias).then_inc(ld_rel, 16)
            link(pool.memset(flip[:, :], 0.0))
            tri(flip, 1.0, ALU.not_equal, 1 - P, 1, 1)
            link(pool.memset(ident[:, :], 0.0))
            tri(ident, 1.0, ALU.not_equal, 0, 1, -1)
            link(pool.memset(identb[:, :], 0.0))
            tri(identb, 1.0, ALU.not_equal, 0, 1, -1)
            link(pool.memset(ones[:, :], 1.0))
            link(pool.memset(negones[:, :], -1.0))
            link(pool.memset(negtri[:, :], -1.0))
            tri(negtri, 0.0, ALU.is_ge, 0, 1, -1)
            link(pool.memset(before[:, :], 1.0))
            tri(before, 0.0, ALU.is_gt, 0, -1, 1)
            link(pool.memset(neg_ge[:, :], BIG_NEG))
            tri(neg_ge, 0.0, ALU.is_ge, 0, 1, -1)
            link(pool.memset(neg_gt[:, :], BIG_NEG))
            tri(neg_gt, 0.0, ALU.is_gt, 0, -1, 1)
            link(pool.memset(epsc[:, :], EPS))
            pool.iota(iota[:, :], pattern=[[1, P]], base=0, channel_multiplier=0,
                      allow_small_or_imprecise_dtypes=True).then_inc(const_ready, 1)
            pool.dma_start(qkg[:, 0:DH], q_norm_g.partition_broadcast(P).rearrange("p a d -> p (a d)")).then_inc(ld_small, 16)
            pool.dma_start(qkg[:, DH:2 * DH], k_norm_g.partition_broadcast(P).rearrange("p a d -> p (a d)")).then_inc(ld_small, 16)
            pool.dma_start(rw[:, :, :], router_w.rearrange("(k p) e -> p k e", p=P)).then_inc(ld_small, 16)
            pool.dma_start(rb[:, :], router_b.partition_broadcast(P)).then_inc(ld_small, 16)
            pool.wait_ge(bias_sb, 1)
            pool.dma_start(bias_d, bv_sb[0:HEADS, :]).then_inc(st_bias, 16)
            pool.wait_ge(st_bias, 16)
            pool.dma_start(toep_r[:, :, :], bass.AP(tensor=bias_d.tensor, offset=0,
                                                    ap=[[1, P], [BIAS_LEN, HEADS], [1, S]])).then_inc(ld_toepR, 16)
            pool.wait_ge(toep_sb, HEADS)
            pool.dma_start(toep_d, toep_f[:, :, :]).then_inc(st_toep, 16)
            for part in (1, 2):
                pool.wait_ge(seg_ready, seg_done(f"ada{part - 1}", 3))
                link(pool.memset(acc[:, :], 0.0))
                pool.dma_start(acc[0:1, :], b_ada[:, part * 2 * D:(part + 1) * 2 * D]).then_inc(ld_bada, 16)
                if part == 2:
                    pool.wait_ge(evac[0], half_before("ada1") + 4)
                    pool.dma_start(mod_d[0], modrow[0:1, :]).then_inc(st_mod, 16)
            pool.wait_ge(evac[1], half_before("ada2") + 4)
            pool.dma_start(mod_d[1], modrow[0:1, :]).then_inc(st_mod, 16)

            for i in range(1, NT):
                pool.wait_ge(score_ok, HEADS * i)
                cut = score[(i - 1) % 2][:, P * i:P * i + P]
                pool.affine_select(out=cut, in_=cut, compare_op=ALU.is_ge, fill=FUTURE, base=0,
                                   pattern=[[-1, P]], channel_multiplier=1).then_inc(score_cut, 1)
                if i == 2:
                    pool.wait_ge(st_toep, 16)
                    pool.wait_ge(side_ps, 1 + max(n for n, t in enumerate(SIDE) if t[0] == "tr"))
                    pool.dma_start(toep[0][:, :, :], toep_d[:, 0:4]).then_inc(ld_toepA, 16)
            pool.wait_ge(s_ps, len(STEPS))
            pool.dma_start(toep[1][:, :, :], toep_d[:, 4:8]).then_inc(ld_toepB, 16)
            pool.wait_ge(l_sb, len(UNITS))
            pool.wait_ge(st_mod, 32)
            pool.dma_start(xres[:, :, :], x[0].rearrange("(t p) d -> p t d", p=P)).then_inc(ld_x2, 16)
            pool.dma_start(gate1[:, :], mod_d[0][:, 0:D].partition_broadcast(P).rearrange("p a d -> p (a d)")).then_inc(ld_g1, 16)
            pool.wait_ge(seg_ready, seg_done("ob1", 3))
            for dst, src in ((shift2, mod_d[0][:, D:2 * D]), (amp2, mod_d[1][:, 0:D]), (g2row, norm2_g)):
                pool.dma_start(dst[:, :], src.partition_broadcast(P).rearrange("p a d -> p (a d)")).then_inc(ld_r2, 16)
            pool.wait_ge(moe_over, 1)
            pool.dma_start(gate2[:, :], mod_d[1][:, D:2 * D].partition_broadcast(P).rearrange("p a d -> p (a d)")).then_inc(ld_g2, 16)

        @block.tensor
        def _(pe):
            def split_ready(n):
                pe.wait_ge(chunk_split, n + 1)

            def three(o, a, b, start, stop):
                pe.matmul(o, a[0], b[1], start=start, stop=False)
                pe.matmul(o, a[1], b[0], start=False, stop=False)
                return pe.matmul(o, a[0], b[0], start=False, stop=stop)

            def wpart(w, k, n0, n1):
                s_ = w % SPL
                return (w_hi[s_][:, 512 * k + n0:512 * k + n1], w_lo[s_][:, 512 * k + n0:512 * k + n1])

            def seg(name, X):
                stationary = SEGS[seg_at[name]][2]
                if half_before(name):
                    pe.wait_ge(evac[SEGS[seg_at[name]][1]], half_before(name))
                raws = first[name]
                for ci, n in enumerate(raws):
                    split_ready(n)
                    for m in range(4):
                        for k in range(4):
                            kk = 4 * ci + k
                            go, end = ci == 0 and k == 0, ci == len(raws) - 1 and k == 3
                            xs = slice(0, S) if stationary else slice(P * m, P * m + P)
                            xx = tuple(part[:, kk, xs] for part in X)
                            if stationary:
                                last = three(bank(name, m)[:, :], wpart(w_of[n], k, P * m, P * m + P), xx, go, end)
                            else:
                                last = three(bank(name, m)[:, :], xx, wpart(w_of[n], k, 0, 512), go, end)
                        if ci == len(raws) - 1:
                            last.then_inc(seg_ready, 1)
                        elif m == 3:
                            last.then_inc(w_used, 1)

            def ada_seg(part):
                name = f"ada{part}"
                if half_before(name):
                    pe.wait_ge(evac[SEGS[seg_at[name]][1]], half_before(name))
                pe.wait_ge(chunk_split, first[name][-1] + 1)
                for m in range(4):
                    pe.matmul(bank(name, m)[:, :], ones[:, :], acc[:, 512 * m:512 * m + 512],
                              start=True, stop=True).then_inc(seg_ready, 1)

            pe.wait_ge(const_ready, 1)
            pe.wait_ge(ld_rel, 32)
            pe.matmul(ps[6][0:HEADS, 0:512], rel_sb[0:BUCKETS, :], oh_sb[0:BUCKETS, 0:512], start=True, stop=True)
            pe.matmul(ps[7][0:HEADS, 0:BIAS_LEN - 512], rel_sb[0:BUCKETS, :], oh_sb[0:BUCKETS, 512:BIAS_LEN],
                      start=True, stop=True).then_inc(bias_ps, 1)
            pe.wait_ge(ld_toepR, 16)
            for h in range(HEADS):
                if h >= 4:
                    pe.wait_ge(toep_sb, h - 3)
                pe.matmul(ps[h % 4][:, :], flip[:, :], toep_r[:, h, :], start=True, stop=True).then_inc(toep_ps, 1)
            pe.wait_ge(toep_sb, HEADS)
            ada_seg(0)
            for tt in range(NT):
                pe.wait_ge(h_rows, tt + 1)
                for g in range(2):
                    n = 2 * tt + g
                    if n == 0:
                        pe.wait_ge(bias_sb, 1)
                    if n >= 4:
                        pe.wait_ge(hT_sp, n - 3)
                    for k in range(4):
                        last = pe.transpose(ps[4 + n % 4][:, P * k:P * k + P],
                                            hn[tt % 2][:, 512 * g + P * k:512 * g + P * k + P], ident[:, :])
                    last.then_inc(hT_ps, 1)
            pe.wait_ge(hT_sp, 2 * NT)
            H = (act_hi, act_lo)
            seg("qa", H)
            seg("ka", H)
            seg("va", H)
            seg("qi", H)
            ada_seg(1)
            pe.wait_ge(evac[1], half_before("misc"))
            ma, mb = first["misc"]
            split_ready(mb)

            def misc_group(o, n0, n1, tt):
                for kk in range(KD):
                    w = w_of[(ma, mb)[kk // 4]]
                    if tt is None:
                        last = three(o, wpart(w, kk % 4, n0, n1), tuple(x_[:, kk, :] for x_ in H), kk == 0, kk == KD - 1)
                    else:
                        last = three(o, tuple(x_[:, kk, P * tt:P * tt + P] for x_ in H), wpart(w, kk % 4, n0, n1),
                                     kk == 0, kk == KD - 1)
                return last

            misc_group(bank("misc", 0)[:, :], 2 * DH, 4 * DH, None).then_inc(seg_ready, 1)
            for tt in range(NT):
                last = misc_group(bank("misc", 1)[:, P * tt:P * tt + P], 0, 2 * DH, tt)
            last.then_inc(seg_ready, 1)
            for tt in range(NT):
                last = misc_group(bank("misc", 2)[:, HEADS * tt:HEADS * tt + HEADS], 4 * DH, 4 * DH + HEADS, tt)
            last.then_inc(seg_ready, 2)
            seg("qb", H)
            ada_seg(2)

            pe.wait_ge(evac[0], half_before("ga0"))
            pe.wait_ge(evac[1], half_before("oa0"))

            def head(t, h, c0, c1):
                o = DH * (h % 2)
                return t[o:o + DH, h // 2, c0:c1]

            def z(n):
                h, i = STEPS[n]
                if n >= 4:
                    pe.wait_ge(a_ready, n - 3)
                pe.matmul(ps[n % 4][:, 0:S - P * i], head(kaT, h, P * i, P * i + P), head(qaT, h, P * i, S),
                          start=True, stop=False, skip_group_check=True).then_inc(z_ps, 1)

            def suffix(n):
                h, i = STEPS[n]
                pe.wait_ge(sp_ready, n + 1)
                for j in range(NT - 1, i - 1, -1):
                    lhs = negtri if j == i else negones
                    pe.matmul(ps[n % 4][:, P * (j - i):S - P * i], lhs[:, :],
                              spb[h % 2][:, OFF[j]:OFF[j] + S - P * j], start=False, stop=False, skip_group_check=True)
                pe.matmul(ps[n % 4][:, 0:P], identb[:, :], neg_ge[:, :], start=False, stop=True,
                          skip_group_check=True).then_inc(s_ps, 1)

            def av_a(h):
                if h >= 2:
                    pe.wait_ge(oa_sp, h - 1)
                pe.wait_ge(a_ready, NT * (h + 1))
                for i in range(NT):
                    last = pe.matmul(ps[4 + h % 2][:, P * i:S], va[:, i, P * (h // 2):P * (h // 2) + P],
                                     ab[h % 2][:, OFF[i]:OFF[i] + S - P * i], start=(i == 0), stop=(i == NT - 1),
                                     skip_group_check=True)
                last.then_inc(oa_ps, 1)

            n_side = [0]

            def side_task(kind, a, h):
                n = n_side[0]
                n_side[0] += 1
                if n >= 2:
                    pe.wait_ge(side_sb, n - 1)
                o = ps[6 + n % 2]
                if kind == "idx":
                    last = pe.matmul(o[:, 0:P * (a + 1)], head(qiT, h, P * a, P * a + P),
                                     kiT[DH * (h % 2):DH * (h % 2) + DH, 0:P * (a + 1)], start=True, stop=True)
                else:
                    pe.wait_ge(qk_norm, 1)
                    for tt in range(NT):
                        last = pe.transpose(o[:, P * tt:P * tt + P],
                                            qkn[:, tt, 2 * a:2 * a + 2].rearrange("p h d -> p (h d)"), ident[:, :])
                last.then_inc(side_ps, 1)

            z(0)
            z(1)
            for n, (h, i) in enumerate(STEPS):
                for t in side[n]:
                    side_task(*t)
                if n + 2 < len(STEPS):
                    z(n + 2)
                suffix(n)
                if h >= 1 and i == 2:
                    av_a(h - 1)
            AVB = {u + 2: (UNITS[u][0], UNITS[u][1] // 4) for u in range(len(UNITS)) if UNITS[u][1] % 4 == 3}

            def logits(u):
                i, h = UNITS[u]
                n = P * (i + 1)
                if u >= 3:
                    pe.wait_ge(l_sb, u - 2)
                if h == 0 and i > 0:
                    pe.wait_ge(mask_ready, i)
                o = ps[u % 3][:, 0:n]
                pe.matmul(o, head(qbT, h, P * i, P * i + P), kbT[DH * (h % 2):DH * (h % 2) + DH, 0:n],
                          start=True, stop=False, skip_group_check=True)
                m = masks[:, i, 0:n] if i else neg_gt[:, :]
                pe.matmul(o, identb[:, :], m, start=False, stop=True, skip_group_check=True).then_inc(l_ps, 1)

            def turn(u):
                i, h = UNITS[u]
                pe.wait_ge(p_norm, u + 1)
                if u >= 2:
                    pe.wait_ge(pT_sb, u - 1)
                for b in range(i + 1):
                    last = pe.transpose(ps[3 + u % 2][:, P * b:P * b + P], lrow[u % 4][:, P * b:P * b + P], ident[:, :])
                last.then_inc(pT_ps, 1)

            def av_b(i, g):
                n = 2 * i + g
                pe.wait_ge(pT_sb, 4 * (n + 1))
                if n >= 2:
                    pe.wait_ge(ob_sp, 2 * (n - 1))
                for b in range(i + 1):
                    last = pe.matmul(ps[5 + n % 2][:, :], vb[:, b, :], pT[n % 2][:, b, :], start=(b == 0), stop=(b == i))
                last.then_inc(ob_ps, 1)

            pe.wait_ge(a_ready, len(STEPS))
            pe.wait_ge(side_sb, len(SIDE))
            logits(0)
            logits(1)
            av_a(HEADS - 1)
            pe.wait_ge(oa_sp, HEADS)
            for u in range(len(UNITS) + 3):
                if u + 2 < len(UNITS):
                    logits(u + 2)
                if u < len(UNITS):
                    turn(u)
                if u in AVB:
                    av_b(*AVB[u])

            pe.wait_ge(l_sb, len(UNITS))
            pe.wait_ge(pT_sb, len(UNITS))
            pe.wait_ge(ob_sp, 2 * 2 * NT)
            for half in range(2):
                seg(f"ga{half}", H)
                seg(f"oa{half}", oaT)
                seg(f"gb{half}", H)
                seg(f"ob{half}", obT)
            pe.wait_ge(m_sp, KD)
            seg("wo0", H)
            seg("wo1", H)

            def turn_rows(tt):
                pe.wait_ge(h2_rows, tt + 1)
                for g in range(2):
                    n = 2 * tt + g
                    if n >= 4:
                        pe.wait_ge(h2T_sb, n - 3)
                    for k in range(4):
                        last = pe.transpose(ps[n % 4][:, P * k:P * k + P],
                                            h2f[tt][:, 512 * g + P * k:512 * g + P * k + P], ident[:, :])
                    last.then_inc(h2T_ps, 1)

            def router(tt):
                pe.wait_ge(h2T_sb, 2 * tt + 2)
                for k in range(KD):
                    last = pe.matmul(ps[4][:, N_EXP * tt:N_EXP * tt + N_EXP], h2T[:, k, P * tt:P * tt + P], rw[:, k, :],
                                     start=(k == 0), stop=(k == KD - 1))
                last.then_inc(r_ps, 1)

            pe.wait_ge(evac[0], half_before("wo0") + 4)
            turn_rows(0)
            pe.wait_ge(ld_small, 64)
            pe.wait_ge(evac[1], half_before("wo1") + 1)
            for tt in range(1, NT):
                turn_rows(tt)
                router(tt - 1)
            router(NT - 1)
            pe.wait_ge(r_sel, 1)
            for tt in range(NT):
                o = ps[5][:, N_EXP * tt:N_EXP * tt + N_EXP]
                for t2 in range(tt):
                    pe.matmul(o, ones[:, :], comb[:, t2, :], start=(t2 == 0), stop=False)
                last = pe.matmul(o, before[:, :], comb[:, tt, :], start=(tt == 0), stop=True)
            for tt in range(NT):
                last = pe.matmul(ps[6][:, 0:N_EXP], ones[:, :], comb[:, tt, :], start=(tt == 0), stop=(tt == NT - 1))
            last.then_inc(pos_ps, 1)

            def gather(X, units):
                for u in units:
                    if u == 0:
                        pe.wait_ge(sel_ready, X + 2)
                    if not isinstance(X, int) or X > 0 or u >= 2:
                        pe.wait_ge(hg_sp, 2 * X + u - 1)
                    for kk in (2 * u, 2 * u + 1):
                        for tt in range(NT):
                            for n, part in enumerate((h2_hi, h2_lo)):
                                last = pe.matmul(ps[2 + u % 2][:, 2 * P * (kk % 2):2 * P * (kk % 2) + 2 * P],
                                                 part[:, tt, P * kk:P * kk + P], sel[:, tt, :, :],
                                                 start=(tt == 0 and n == 0), stop=(tt == NT - 1 and n == 1))
                    last.then_inc(hg_ps, 1)

            def turn_sel(X, b):
                if b == 0:
                    pe.wait_ge(ws_sb, X + 2)
                else:
                    pe.wait_ge(selT_sb, X)
                for tt in range(NT):
                    last = pe.transpose(ps[7][:, P * tt:P * tt + P], sel[:, tt, b, :].bitcast(F32), ident[:, :])
                last.then_inc(selT_ps, 1)

            def slot_weights(X, e):
                if not isinstance(X, int) or X >= 2:
                    pe.wait_ge(selT_sb, X)
                for b in range(2):
                    for tt in range(NT):
                        last = pe.matmul(ps[7][:, b:b + 1], sel[:, tt, b, :].bitcast(F32),
                                         comb[:, tt, bass.ds(e + b, 1)], start=(tt == 0), stop=(tt == NT - 1))
                last.then_inc(ws_ps, 2)

            def scatter(X, ks):
                for k in ks:
                    tt, n = k // 2, k % 2
                    if k == 0:
                        pe.wait_ge(selT_sb, X + 2)
                        pe.wait_ge(y_sp, 2 * X + 4)
                    if k >= 2:
                        pe.wait_ge(yadd, 4 * X + k - 1)
                    o = ps[5 + k % 2][:, :]
                    for b in range(2):
                        pe.matmul(o, selT[b][:, tt, :], ye_lo[b][:, 512 * n:512 * n + 512], start=(b == 0), stop=False)
                        last = pe.matmul(o, selT[b][:, tt, :], ye_hi[b][:, 512 * n:512 * n + 512], start=False,
                                         stop=(b == 1))
                    last.then_inc(sc_ps, 1)

            def expert(X, e, b, first_, last_):
                fresh = isinstance(X, int) and X == 0
                for cc in range(4):
                    pe.wait_ge(chunk_split, EC * X + cc + 1 + N_RAW)
                    s_ = (EC * b + cc) % E_SPL
                    if cc == 0:
                        pe.wait_ge(hg_sp, 2 * (X - b) + 4)
                        if not fresh:
                            pe.wait_ge(silu_ok, X)
                    if cc == 2 and not fresh:
                        pe.wait_ge(hid_ok, X)
                    for k in range(4):
                        kk = 4 * (cc % 2) + k
                        m = three(ps[cc // 2][:, :], (hgT_hi[:, b, kk, :], hgT_lo[:, b, kk, :]),
                                  (e_hi[s_][:, 512 * k:512 * k + 512], e_lo[s_][:, 512 * k:512 * k + 512]),
                                  kk == 0, kk == KD - 1)
                    m.then_inc((w_used, g_ps, w_used, u_ps)[cc], 1)
                    if not first_ and b == 0 and cc > 0:
                        scatter(X - 2, (2 * cc - 2, 2 * cc - 1))
                if b == 0:
                    if not first_:
                        scatter(X - 2, (6, 7))
                elif not last_:
                    gather(X + 1, (0, 1))
                pe.wait_ge(hid_ok, X + 1)
                if not fresh:
                    pe.wait_ge(hidT_sp, X)
                for f in range(4):
                    t = pe.transpose(ps[4][:, P * f:P * f + P], hid[:, P * f:P * f + P], ident[:, :])
                t.then_inc(hidT_ps, 1)
                if b == 0:
                    turn_sel(X, 0)
                    turn_sel(X + 1, 1)
                elif not last_:
                    slot_weights(X + 1, e + 1)
                    gather(X + 1, (2, 3))
                pe.wait_ge(hidT_sp, X + 1)
                if b == 1:
                    pe.wait_ge(y_sp, 2 * X)
                elif not fresh:
                    pe.wait_ge(yadd, 4 * X)
                for cc in range(4, 6):
                    pe.wait_ge(chunk_split, EC * X + cc + 1 + N_RAW)
                    s_ = (EC * b + cc) % E_SPL
                    for n in range(2):
                        for k in range(2):
                            f = 2 * (cc - 4) + k
                            a = D * k + 512 * n
                            m = three(ps[5 + n][:, :], (hidT_hi[:, f, :], hidT_lo[:, f, :]),
                                      (e_hi[s_][:, a:a + 512], e_lo[s_][:, a:a + 512]), f == 0, f == 3)
                    m.then_inc((w_used, y_ps)[cc - 4], 1)

            def expert_pass(X0):
                gather(X0, (0, 1))
                slot_weights(X0, 0)
                gather(X0, (2, 3))
                expert(X0, 0, 0, True, False)
                expert(X0 + 1, 1, 1, False, False)
                with pe.Fori(1, N_EXP // 2 - 1) as q:
                    expert(X0 + q * 2, q * 2, 0, False, False)
                    expert(X0 + q * 2 + 1, q * 2 + 1, 1, False, False)
                expert(X0 + N_EXP - 2, N_EXP - 2, 0, False, False)
                expert(X0 + N_EXP - 1, N_EXP - 1, 1, False, True)
                scatter(X0 + N_EXP - 2, range(8))

            pe.wait_ge(h2_sp, NT)
            expert_pass(0)
            pe.wait_ge(route_ok, 1)
            more = pe.value_load(over[0:1, 0:1], min_val=0, max_val=1)
            with pe.If(more > 0):
                with pe.Fori(1, PASSES) as p:
                    pe.wait_ge(yadd, p * (4 * N_EXP))
                    expert_pass(p * N_EXP)
                pe.nop()

        @block.scalar
        def _(act):
            n_chain = [0]

            def link(ins):
                n_chain[0] += 1
                ins.then_inc(act_chain, 1)
                act.wait_ge(act_chain, n_chain[0])

            def high(n):
                w = w_of[n]
                act.wait_ge(raw_in[n % RAW], fill[n])
                if w >= SPL:
                    kind, value = used[w - SPL]
                    act.wait_ge(seg_ready if kind == "seg" else w_used, value)
                nk = 4
                top = max(b for _, b, _ in chunks[n][2])
                act.activation(cols(w_hi[w % SPL], 0, top, nk), cols(raw[n % RAW], 0, top, nk), ACT.Copy
                               ).then_inc(hi_ready, 1)

            act.wait_ge(ld_c, 16)
            act.activation(sc_col[:, :], c_col[:, :], ACT.Silu).then_inc(sc_ready, 1)
            act.wait_ge(bias_ps, 1)
            act.activation(bv_sb[0:HEADS, 0:512], ps[6][0:HEADS, 0:512], ACT.Copy)
            act.activation(bv_sb[0:HEADS, 512:BIAS_LEN], ps[7][0:HEADS, 0:BIAS_LEN - 512], ACT.Copy).then_inc(bias_sb, 1)
            for h in range(HEADS):
                act.wait_ge(toep_ps, h + 1)
                act.activation(toep_f[:, h, :], ps[h % 4][:, :], ACT.Copy).then_inc(toep_sb, 1)
            act.wait_ge(ld_x, 16)
            for tt in range(NT):
                act.activation(hn[tt % 2][:, :], xres[:, tt, :], ACT.Square, accum_out=st[:, tt, 0:1]).then_inc(h_ss, 1)
                if tt < NT - 1:
                    act.wait_ge(h_ss, tt + 1)
            act.wait_ge(h_ss, NT)
            act.wait_ge(const_ready, 1)
            act.activation(st[:, :, 1:2], st[:, :, 0:1], ACT.Sqrt, bias=epsc[:, 0:1], scale=1.0 / D).then_inc(h_rs, 1)
            raws = [n for n in range(N_RAW) if n in w_of]
            todo = iter(raws)
            for _ in range(2):
                high(next(todo))
            for m in range(2):
                act.wait_ge(seg_ready, seg_done("ada0", m))
                act.activation(shift1[:, 512 * m:512 * m + 512], bank("ada0", m)[:, :], ACT.Copy).then_inc(evac[0], 1)
            for n in range(2 * NT):
                act.wait_ge(hT_ps, n + 1)
                tt, g = n // 2, n % 2
                act.activation(act_hi[:, 4 * g:4 * g + 4, P * tt:P * tt + P],
                               ps[4 + n % 4][:, :].rearrange("p (k s) -> p k s", k=4), ACT.Copy).then_inc(hT_hi, 1)

            high(next(todo))

            def seg_copy(name, dst, scale=1.0):
                half = SEGS[seg_at[name]][1]
                for m in range(4):
                    act.wait_ge(seg_ready, seg_done(name, m))
                    act.activation(dst[:, m, :], bank(name, m)[:, :], ACT.Copy, scale=scale).then_inc(evac[half], 1)

            for name, dst, scale in (("qa", qaT, SCALE), ("ka", kaT, 1.0), ("va", va, 1.0), ("qi", qiT, 1.0)):
                high(next(todo))
                if name == "qa":
                    act.wait_ge(st_toep, 16)
                seg_copy(name, dst, scale)
                high(next(todo))
            def mod_rows(part):
                name = f"ada{part}"
                if part == 1:
                    act.wait_ge(h_rows, NT)
                else:
                    act.wait_ge(st_mod, 16)
                for m in range(4):
                    act.wait_ge(seg_ready, seg_done(name, m))
                    act.activation(modrow[0:1, 512 * m:512 * m + 512], bank(name, m)[0:1, :], ACT.Copy
                                   ).then_inc(evac[SEGS[seg_at[name]][1]], 1)

            mod_rows(1)
            high(next(todo))
            act.wait_ge(seg_ready, seg_done("misc", 0))
            act.activation(kiT[:, :], bank("misc", 0)[:, :], ACT.Copy).then_inc(evac[1], 1)
            act.wait_ge(seg_ready, seg_done("misc", 1))
            kv = bank("misc", 1)[:, :].rearrange("p (t n) -> p t n", t=NT)
            for r in range(2):
                act.activation(vb[:, :, DH * r:DH * r + DH], kv[:, :, DH:2 * DH], ACT.Copy)
                last = act.activation(qkn[:, :, 8 + r, :], kv[:, :, 0:DH], ACT.Copy)
            last.then_inc(evac[1], 1)
            act.wait_ge(seg_ready, seg_done("misc", 3))
            act.activation(wi[:, :, :], bank("misc", 2)[:, 0:NT * HEADS].rearrange("p (t n) -> p t n", t=NT), ACT.Copy
                           ).then_inc(evac[1], 2)
            high(next(todo))
            for m in range(4):
                act.wait_ge(seg_ready, seg_done("qb", m))
                act.activation(qkn[:, m, 0:8, :].rearrange("p h d -> p (h d)"), bank("qb", m)[:, :], ACT.Copy
                               ).then_inc(evac[0], 1)
            high(next(todo))
            mod_rows(2)
            act.wait_ge(qk_var, 1)
            act.activation(st[:, :, :], st[:, :, :], ACT.Sqrt, bias=epsc[:, 0:1], scale=1.0 / DH).then_inc(qk_sd, 1)

            n_side = [0]

            def side_task(kind, a, h):
                n = n_side[0]
                n_side[0] += 1
                act.wait_ge(side_ps, n + 1)
                o = ps[6 + n % 2]
                if kind == "idx":
                    k = HEADS * (a - 1) + h
                    if k >= 2:
                        act.wait_ge(score_ok, k - 1)
                    act.activation(rel[k % 2][:, 0:P * (a + 1)], o[:, 0:P * (a + 1)], ACT.Relu).then_inc(side_sb, 1)
                else:
                    dst = qbT[:, a, :] if a < 4 else kbT[:, :]
                    act.activation(dst, o[:, :], ACT.Copy, scale=SCALE if a < 4 else 1.0).then_inc(side_sb, 1)

            def soft(n):
                h, i = STEPS[n]
                w = S - P * i
                t = sig[n % 2][:, 0:w]
                act.wait_ge(z_ps, n + 1)
                if n >= 2:
                    act.wait_ge(sp_ready, n - 1)
                link(act.activation(t, ps[n % 4][:, 0:w], ACT.Abs))
                link(act.activation(t, t, ACT.Exp, scale=-1.0))
                act.activation(t, t, ACT.Ln, bias=1.0).then_inc(z_soft, 1)

            def weights(n):
                h, i = STEPS[n]
                act.wait_ge(s_ps, n + 1)
                if h >= 2:
                    act.wait_ge(oa_ps, h - 1)
                act.activation(ab[h % 2][:, OFF[i]:OFF[i] + S - P * i], ps[n % 4][:, 0:S - P * i], ACT.Exp
                               ).then_inc(a_ready, 1)

            def oa_high(h):
                act.wait_ge(oa_ps, h + 1)
                o = DH * (h % 2)
                act.activation(oaT[0][o:o + DH, h // 2, :], ps[4 + h % 2][o:o + DH, :], ACT.Copy).then_inc(oa_hi, 1)

            act.wait_ge(st_mod, 32)
            act.preload_act_table_set("natural_log_exp_and_others")
            soft(0)
            for n, (h, i) in enumerate(STEPS):
                for t in side[n]:
                    side_task(*t)
                if n + 1 < len(STEPS):
                    soft(n + 1)
                weights(n)
                if h >= 1 and i == 1:
                    oa_high(h - 1)
            def exps(u):
                i, h = UNITS[u]
                w = P * (i + 1)
                act.wait_ge(l_sb, u + 1)
                act.activation(lrow[u % 4][:, 0:w], lrow[u % 4][:, 0:w], ACT.Exp, bias=nmax[:, u % 4:u % 4 + 1],
                               accum_out=rsum[:, u % 4:u % 4 + 1]).then_inc(p_exp, 1)

            def pT_copy(u):
                i, h = UNITS[u]
                n = u // 4
                act.wait_ge(pT_ps, u + 1)
                if n >= 2:
                    act.wait_ge(ob_ps, n - 1)
                act.activation(pT[n % 2][:, 0:i + 1, P * (h % 4):P * (h % 4) + P],
                               ps[3 + u % 2][:, 0:P * (i + 1)].rearrange("p (b s) -> p b s", b=i + 1), ACT.Copy
                               ).then_inc(pT_sb, 1)

            def ob_high(n):
                i, g = n // 2, n % 2
                act.wait_ge(ob_ps, n + 1)
                for r in range(2):
                    o = DH * r
                    act.activation(obT[0][o:o + DH, 2 * g:2 * g + 2, P * i:P * i + P],
                                   ps[5 + n % 2][o:o + DH, :].rearrange("p (e r s) -> p e r s", e=2, r=2)[:, :, r, :],
                                   ACT.Copy).then_inc(ob_hi, 1)

            exps(0)
            oa_high(HEADS - 1)
            for u in range(len(UNITS) + 4):
                if u + 1 < len(UNITS):
                    exps(u + 1)
                if u < len(UNITS):
                    pT_copy(u)
                if u >= 6 and (u - 6) % 4 == 0 and (u - 6) // 4 < 2 * NT:
                    ob_high((u - 6) // 4)

            def gate_sig(name):
                k = {"a": 0, "b": 1}[name[1]]
                half = SEGS[seg_at[name]][1]
                nth = 2 * int(name[2]) + k
                for m in range(4):
                    act.wait_ge(seg_ready, seg_done(name, m))
                    if nth >= 2:
                        act.wait_ge(evac[1], half_before(f"o{name[1]}0") + 4)
                    act.activation(gsig[k][:, m, :], bank(name, m)[:, :], ACT.Sigmoid).then_inc(evac[half], 1)

            for half in range(2):
                for name in (f"ga{half}", f"oa{half}", f"gb{half}", f"ob{half}"):
                    for _ in first[name]:
                        nxt = next(todo, None)
                        if nxt is not None:
                            high(nxt)
                    if name[0] == "g":
                        gate_sig(name)
            for k in range(KD):
                act.wait_ge(merged_ok, k + 1)
                act.wait_ge(seg_ready, seg_done("gb1", 3))
                act.activation(act_hi[:, k, :], merged[:, k, :], ACT.Copy).then_inc(m_hi, 1)
            for nxt in todo:
                high(nxt)
            def mean_square(tt):
                act.wait_ge(x1_ready, NT + tt + 1)
                if tt:
                    act.wait_ge(h2_ss, tt)
                act.activation(junk[:, :], xres[:, tt, :], ACT.Square, accum_out=st[:, tt, 2:3]).then_inc(h2_ss, 1)
                act.wait_ge(h2_ss, tt + 1)
                act.activation(st[:, tt, 3:4], st[:, tt, 2:3], ACT.Sqrt, bias=epsc[:, 0:1], scale=1.0 / D
                               ).then_inc(h2_sd, 1)

            def rows_high(tt):
                act.wait_ge(h2_rows, tt + 1)
                if tt == 2:
                    act.wait_ge(seg_ready, seg_done("wo1", 3))
                act.activation(h2_hi[:, tt, :], h2f[tt][:, :], ACT.Copy).then_inc(h2_hiR, 1)

            def rows_turned(tt):
                for g in range(2):
                    n = 2 * tt + g
                    act.wait_ge(h2T_ps, n + 1)
                    act.activation(h2T[:, 4 * g:4 * g + 4, P * tt:P * tt + P],
                                   ps[n % 4][:, :].rearrange("p (k s) -> p k s", k=4), ACT.Copy).then_inc(h2T_sb, 1)

            mean_square(0)
            mean_square(1)
            for tt in range(NT):
                rows_high(tt)
                if tt + 2 < NT:
                    mean_square(tt + 2)
                if tt:
                    rows_turned(tt - 1)
            rows_turned(NT - 1)

            def high_e(X, cc, b):
                z_ = EC * b + cc
                s_ = z_ % E_SPL
                act.wait_ge(raw_in[z_ % E_RAW], slot_count[z_ % E_RAW] + 32 * (X - b) + 16 * (z_ // E_RAW + 1))
                if cc >= 4:
                    act.wait_ge(*((w_used, N_USED + 3 * X + 1), (g_ps, X + 1))[cc - 4])
                elif not isinstance(X, int) or X >= 1:
                    act.wait_ge(*((w_used, N_USED + 3 * X - 1), (u_ps, X), (w_used, N_USED + 3 * X), (y_ps, X))[cc])
                elif cc < SPL:
                    kind, value = used[max(w for w in range(N_W) if w % SPL == cc)]
                    act.wait_ge(seg_ready if kind == "seg" else w_used, value)
                else:
                    act.wait_ge(chunk_split, N_RAW)
                act.activation(e_hi[s_][:, :], raw[z_ % E_RAW][:, :], ACT.Copy).then_inc(hi_ready, 1)

            for cc in range(3):
                high_e(0, cc, 0)
            for tt in range(NT):
                act.wait_ge(r_lg, 1)
                act.activation(comb[:, tt, :], comb[:, tt, :], ACT.Exp, bias=nmax[:, tt:tt + 1],
                               accum_out=rsum[:, tt:tt + 1]).then_inc(r_exp, 1)

            def y_high(X, b):
                act.wait_ge(y_ps, X + 1)
                if not isinstance(X, int) or X >= 2:
                    act.wait_ge(sc_ps, 4 * (X - b))
                for n in range(2):
                    act.activation(ye_hi[b][:, 512 * n:512 * n + 512], ps[5 + n][:, :], ACT.Copy).then_inc(y_hi, 1)

            def hg_high(X, u):
                act.wait_ge(hg_ps, 2 * X + u + 1)
                act.activation(hgT_hi[:, :, 2 * u:2 * u + 2, :].rearrange("p b k s -> p k b s"),
                               ps[2 + u % 2][:, :].rearrange("p (k b s) -> p k b s", k=2, b=2), ACT.Copy).then_inc(hg_hi, 1)

            def selT_copy(X, b):
                act.wait_ge(selT_ps, X + 1)
                if not isinstance(X, int) or X >= 2:
                    act.wait_ge(sc_ps, 4 * (X - b))
                act.activation(selT[b][:, :, :], ps[7][:, :].rearrange("p (t s) -> p t s", t=NT), ACT.Copy
                               ).then_inc(selT_sb, 1)

            def weight_copy(X):
                act.wait_ge(ws_ps, X + 2)
                if not isinstance(X, int) or X >= 2:
                    act.wait_ge(hid_ok, X)
                act.activation(slot_w[:, :], ps[7][:, 0:2], ACT.Copy).then_inc(ws_sb, 2)

            def expert(X, b, first_, last_):
                if not first_:
                    y_high(X - 1, 1 - b)
                high_e(X, 3, b)
                high_e(X, 4, b)
                act.wait_ge(g_ps, X + 1)
                if not isinstance(X, int) or X >= 1:
                    act.wait_ge(hid_ok, X)
                act.activation(silu[:, :], ps[0][:, :], ACT.Silu).then_inc(silu_ok, 1)
                high_e(X, 5, b)
                if not last_:
                    high_e(X + 1, 0, 1 - b)
                if b == 1 and not last_:
                    hg_high(X + 1, 0)
                    hg_high(X + 1, 1)
                act.wait_ge(hidT_ps, X + 1)
                if not isinstance(X, int) or X >= 1:
                    act.wait_ge(y_ps, X)
                act.activation(hidT_hi[:, :, :], ps[4][:, :].rearrange("p (k s) -> p k s", k=4), ACT.Copy
                               ).then_inc(hidT_h, 1)
                if b == 0:
                    selT_copy(X, 0)
                    selT_copy(X + 1, 1)
                elif not last_:
                    weight_copy(X + 1)
                    hg_high(X + 1, 2)
                if not last_:
                    high_e(X + 1, 1, 1 - b)
                if b == 1 and not last_:
                    hg_high(X + 1, 3)
                if not last_:
                    high_e(X + 1, 2, 1 - b)

            def expert_pass(X0):
                if not isinstance(X0, int):
                    for cc in range(3):
                        high_e(X0, cc, 0)
                hg_high(X0, 0)
                hg_high(X0, 1)
                weight_copy(X0)
                hg_high(X0, 2)
                hg_high(X0, 3)
                expert(X0, 0, True, False)
                expert(X0 + 1, 1, False, False)
                with act.Fori(1, N_EXP // 2 - 1) as q:
                    expert(X0 + q * 2, 0, False, False)
                    expert(X0 + q * 2 + 1, 1, False, False)
                expert(X0 + N_EXP - 2, 0, False, False)
                expert(X0 + N_EXP - 1, 1, False, True)
                y_high(X0 + N_EXP - 1, 1)

            expert_pass(0)
            act.wait_ge(route_ok, 1)
            more = act.value_load(over[0:1, 0:1], min_val=0, max_val=1)
            with act.If(more > 0):
                with act.Fori(1, PASSES) as p:
                    expert_pass(p * N_EXP)
                act.nop()

        @block.vector
        def _(dve):
            n_chain = [0]

            def link(ins):
                n_chain[0] += 1
                ins.then_inc(dve_chain, 1)
                dve.wait_ge(dve_chain, n_chain[0])

            def low(n):
                w = w_of[n]
                dve.wait_ge(hi_ready, w + 1)
                top = max(b for _, b, _ in chunks[n][2])
                hi, lo, r = (cols(t, 0, top) for t in (w_hi[w % SPL], w_lo[w % SPL], raw[n % RAW]))
                dve.tensor_tensor(lo, r, hi.bitcast(F32), ALU.subtract).then_inc(chunk_split, 1)

            def ada_step(n):
                part, k = int(chunks[n][0][3]), n_ada[0] % KD
                n_ada[0] += 1
                if k == 0:
                    dve.wait_ge(ld_bada, 16 * (part + 1))
                dve.wait_ge(raw_in[n % RAW], fill[n])
                dve.scalar_tensor_tensor(out=acc[:, :], in0=raw[n % RAW][:, :], scalar=sc_col[:, k:k + 1], in1=acc[:, :],
                                         op0=ALU.mult, op1=ALU.add).then_inc(chunk_split, 1)
                dve.wait_ge(chunk_split, n + 1)

            n_ada = [0]
            dve.wait_ge(sc_ready, 1)
            todo = iter(range(N_RAW))

            def raw_chunks(count):
                for _ in range(count):
                    n = next(todo, None)
                    if n is not None:
                        low(n) if n in w_of else ada_step(n)

            raw_chunks(KD)
            dve.wait_ge(h_rs, 1)
            link(dve.reciprocal(st[:, :, 1:2], st[:, :, 1:2]))
            dve.wait_ge(ld_rows, 16)
            for m in range(2, 4):
                dve.wait_ge(seg_ready, seg_done("ada0", m))
                a = 512 * (m - 2)
                dve.scalar_tensor_tensor(out=amp1[:, a:a + 512], in0=bank("ada0", m)[:, :], scalar=1.0,
                                         in1=g1row[:, a:a + 512], op0=ALU.add, op1=ALU.mult).then_inc(evac[0], 1)
            dve.wait_ge(evac[0], 4)
            for tt in range(NT):
                if tt >= 2:
                    dve.wait_ge(hT_ps, 2 * (tt - 1))
                link(dve.scalar_tensor_tensor(out=hn[tt % 2][:, :], in0=xres[:, tt, :], scalar=st[:, tt, 1:2],
                                              in1=amp1[:, :], op0=ALU.mult, op1=ALU.mult))
                dve.tensor_tensor(hn[tt % 2][:, :], hn[tt % 2][:, :], shift1[:, :], ALU.add).then_inc(h_rows, 1)
                if tt >= 1:
                    for g in range(2):
                        n = 2 * (tt - 1) + g
                        dve.wait_ge(hT_hi, n + 1)
                        dst = act_lo[:, 4 * g:4 * g + 4, P * (tt - 1):P * tt]
                        dve.tensor_tensor(dst, ps[4 + n % 4][:, :].rearrange("p (k s) -> p k s", k=4),
                                          act_hi[:, 4 * g:4 * g + 4, P * (tt - 1):P * tt].bitcast(F32), ALU.subtract
                                          ).then_inc(hT_sp, 1)
                if tt == 1:
                    raw_chunks(1)
            for g in range(2):
                n = 2 * (NT - 1) + g
                dve.wait_ge(hT_hi, n + 1)
                dve.tensor_tensor(act_lo[:, 4 * g:4 * g + 4, P * (NT - 1):S],
                                  ps[4 + n % 4][:, :].rearrange("p (k s) -> p k s", k=4),
                                  act_hi[:, 4 * g:4 * g + 4, P * (NT - 1):S].bitcast(F32), ALU.subtract
                                  ).then_inc(hT_sp, 1)
            ada_end = max(n for n in range(N_RAW) if n not in w_of)
            raw_chunks(ada_end + 1 - KD - 1)
            dve.wait_ge(evac[0], half_before("qb") + 4)
            dve.wait_ge(evac[1], half_before("ada2"))
            dve.wait_ge(seg_ready, seg_done("ada2", 3))
            qv = qkn[:, :, :, :].rearrange("p t h d -> p (t h d)")
            link(dve.tensor_tensor(qk_sq[:, :, :, :].rearrange("p t h d -> p (t h d)"), qv, qv, ALU.mult))
            dve.tensor_reduce(st[:, :, :], qk_sq[:, :, :, :], AX.X, ALU.add).then_inc(qk_var, 1)
            dve.wait_ge(qk_sd, 1)
            link(dve.reciprocal(st[:, :, :], st[:, :, :]))
            for tt in range(NT):
                link(dve.tensor_tensor(qkn[:, tt], qkn[:, tt], st[:, tt, :].unsqueeze(2).broadcast_to([P, 10, DH]), ALU.mult))
            dve.wait_ge(ld_small, 64)
            for tt in range(NT):
                dve.tensor_tensor(qkn[:, tt, 0:8], qkn[:, tt, 0:8],
                                  qkg[:, 0:DH].unsqueeze(1).broadcast_to([P, 8, DH]), ALU.mult)
                last = dve.tensor_tensor(qkn[:, tt, 8:10], qkn[:, tt, 8:10],
                                         qkg[:, DH:2 * DH].unsqueeze(1).broadcast_to([P, 2, DH]), ALU.mult)
            last.then_inc(qk_norm, 1)

            def softplus(n):
                h, i = STEPS[n]
                w = S - P * i
                s_ = spb[h % 2][:, OFF[i]:OFF[i] + w]
                dve.wait_ge(z_soft, n + 1)
                if h >= 2:
                    dve.wait_ge(s_ps, NT * (h - 1))
                link(dve.scalar_tensor_tensor(out=s_, in0=ps[n % 4][:, 0:w], scalar=0.0, in1=sig[n % 2][:, 0:w],
                                              op0=ALU.max, op1=ALU.add))
                dve.tensor_tensor(s_[:, 0:P], s_[:, 0:P], before[:, :], ALU.mult).then_inc(sp_ready, 1)

            def oa_low(h):
                o = DH * (h % 2)
                dve.wait_ge(oa_hi, h + 1)
                dve.tensor_tensor(oaT[1][o:o + DH, h // 2, :], ps[4 + h % 2][o:o + DH, :],
                                  oaT[0][o:o + DH, h // 2, :].bitcast(F32), ALU.subtract).then_inc(oa_sp, 1)

            n_side, rounds = [0], []

            def side_task(kind, a, h):
                n = n_side[0]
                n_side[0] += 1
                if kind == "tr":
                    return
                k = HEADS * (a - 1) + h
                w = P * (a + 1)
                sc = score[(a - 1) % 2][:, 0:w]
                dve.wait_ge(side_sb, n + 1)
                if h == 0:
                    dve.tensor_scalar(sc, rel[k % 2][:, 0:w], wi[:, a, h:h + 1], None, ALU.mult).then_inc(score_ok, 1)
                else:
                    dve.scalar_tensor_tensor(out=sc, in0=rel[k % 2][:, 0:w], scalar=wi[:, a, h:h + 1], in1=sc,
                                             op0=ALU.mult, op1=ALU.add).then_inc(score_ok, 1)
                dve.wait_ge(score_ok, k + 1)
                if h == HEADS - 1:
                    rounds.extend((a, r) for r in range(TOPK // 8))

            def topk_round():
                a, r = rounds.pop(0)
                sc = score[(a - 1) % 2][:, 0:P * (a + 1)]
                if r == 0:
                    dve.wait_ge(score_cut, a)
                link(dve.max(m8[r % 2][:, :], sc))
                link(dve.match_replace(sc, m8[r % 2][:, :], sc, TAKEN))
                if r == TOPK // 8 - 1:
                    dve.wait_ge(side_ps, 1 + max(n for n, t in enumerate(SIDE) if t[0] == "tr"))
                    dve.tensor_scalar(masks[:, a, 0:P * (a + 1)], sc, TAKEN, BIG_NEG, ALU.not_equal, ALU.mult
                                      ).then_inc(mask_ready, 1)
                    dve.wait_ge(mask_ready, a)

            for n, (h, i) in enumerate(STEPS):
                softplus(n)
                for t in side[n]:
                    side_task(*t)
                for _ in range(2):
                    if rounds:
                        topk_round()
                if h >= 1 and i == 0:
                    oa_low(h - 1)
            def rows(u):
                i, h = UNITS[u]
                w = P * (i + 1)
                dve.wait_ge(l_ps, u + 1)
                if u >= 4:
                    dve.wait_ge(pT_ps, u - 3)
                if u == 0:
                    dve.wait_ge(ld_toepA, 16)
                if u == 4:
                    dve.wait_ge(ld_toepB, 16)
                a = S - P * (i + 1)
                link(dve.tensor_tensor(lrow[u % 4][:, 0:w], ps[u % 3][:, 0:w], toep[h // 4][:, h % 4, a:a + w], ALU.add))
                dve.tensor_reduce(nmax[:, u % 4:u % 4 + 1], lrow[u % 4][:, 0:w], AX.X, ALU.max, negate=True
                                  ).then_inc(l_sb, 1)

            def normal(u):
                i, h = UNITS[u]
                w = P * (i + 1)
                dve.wait_ge(p_exp, u + 1)
                link(dve.reciprocal(rsum[:, u % 4:u % 4 + 1], rsum[:, u % 4:u % 4 + 1]))
                dve.tensor_scalar(lrow[u % 4][:, 0:w], lrow[u % 4][:, 0:w], rsum[:, u % 4:u % 4 + 1], None, ALU.mult
                                  ).then_inc(p_norm, 1)

            def ob_low(n):
                i, g = n // 2, n % 2
                for r in range(2):
                    o = DH * r
                    dve.wait_ge(ob_hi, 2 * n + r + 1)
                    hi = obT[0][o:o + DH, 2 * g:2 * g + 2, P * i:P * i + P]
                    dve.tensor_tensor(obT[1][o:o + DH, 2 * g:2 * g + 2, P * i:P * i + P],
                                      ps[5 + n % 2][o:o + DH, :].rearrange("p (e r s) -> p e r s", e=2, r=2)[:, :, r, :],
                                      hi.bitcast(F32), ALU.subtract).then_inc(ob_sp, 1)

            dve.wait_ge(a_ready, len(STEPS) )
            dve.wait_ge(oa_ps, HEADS - 1)
            rows(0)
            oa_low(HEADS - 1)
            for u in range(len(UNITS)):
                if rounds and u < HEADS:
                    for _ in range(3):
                        if rounds:
                            topk_round()
                if u + 1 < len(UNITS):
                    rows(u + 1)
                normal(u)
                if u >= 7 and (u - 7) % 4 == 0:
                    ob_low((u - 7) // 4)
            assert not rounds
            for n in range((len(UNITS) - 8) // 4 + 1, 2 * NT):
                ob_low(n)

            def gated(name):
                half, k = int(name[2]), {"a": 0, "b": 1}[name[1]]
                for m in range(4):
                    j = 4 * half + m
                    dve.wait_ge(seg_ready, seg_done(name, m))
                    dve.wait_ge(evac[0], half_before(f"g{name[1]}{half}") + m + 1)
                    if k == 0:
                        dve.tensor_tensor(merged[:, j, :], bank(name, m)[:, :], gsig[0][:, m, :], ALU.mult).then_inc(evac[1], 1)
                        dve.wait_ge(evac[1], half_before(name) + m + 1)
                    else:
                        t = etmp[m % 2][:, :]
                        dve.tensor_tensor(t, bank(name, m)[:, :], gsig[1][:, m, :], ALU.mult).then_inc(evac[1], 1)
                        dve.wait_ge(evac[1], half_before(name) + m + 1)
                        dve.tensor_tensor(merged[:, j, :], merged[:, j, :], t, ALU.add).then_inc(merged_ok, 1)

            for half in range(2):
                raw_chunks(3)
                gated(f"oa{half}")
                raw_chunks(3)
                gated(f"ob{half}")
            for k in range(KD):
                dve.wait_ge(m_hi, k + 1)
                dve.tensor_tensor(act_lo[:, k, :], merged[:, k, :], act_hi[:, k, :].bitcast(F32), ALU.subtract
                                  ).then_inc(m_sp, 1)
            def residual(half, m):
                name = f"wo{half}"
                dve.wait_ge(seg_ready, seg_done(name, m))
                t = etmp[m % 2][:, :]
                a = slice(512 * half, 512 * half + 512)
                dve.tensor_tensor(t, bank(name, m)[:, :], gate1[:, a], ALU.mult).then_inc(evac[half], 1)
                dve.wait_ge(evac[half], half_before(name) + m + 1)
                dve.tensor_tensor(xres[:, m, a], xres[:, m, a], t, ALU.add).then_inc(x1_ready, 1)

            def norm2(tt):
                dve.wait_ge(h2_sd, tt + 1)
                link(dve.reciprocal(st[:, tt, 3:4], st[:, tt, 3:4]))
                t = h2f[tt][:, :]
                link(dve.scalar_tensor_tensor(out=t, in0=xres[:, tt, :], scalar=st[:, tt, 3:4], in1=amp2[:, :],
                                              op0=ALU.mult, op1=ALU.mult))
                dve.tensor_tensor(t, t, shift2[:, :], ALU.add).then_inc(h2_rows, 1)

            raw_chunks(2)
            dve.wait_ge(ld_x2, 16)
            dve.wait_ge(ld_g1, 16)
            for m in range(4):
                residual(0, m)
            raw_chunks(2)
            dve.wait_ge(ld_r2, 48)
            link(dve.scalar_tensor_tensor(out=amp2[:, :], in0=amp2[:, :], scalar=1.0, in1=g2row[:, :],
                                          op0=ALU.add, op1=ALU.mult))
            residual(1, 0)
            for tt in range(NT):
                if tt + 1 < NT:
                    residual(1, tt + 1)
                norm2(tt)
            for tt in range(NT):
                dve.wait_ge(h2_hiR, tt + 1)
                dve.tensor_tensor(h2_lo[:, tt, :], h2f[tt][:, :], h2_hi[:, tt, :].bitcast(F32), ALU.subtract
                                  ).then_inc(h2_sp, 1)
            def low_e(X, cc, b):
                z_ = EC * b + cc
                s_ = z_ % E_SPL
                dve.wait_ge(hi_ready, N_W + EC * X + cc + 1)
                dve.tensor_tensor(e_lo[s_][:, :], raw[z_ % E_RAW][:, :], e_hi[s_][:, :].bitcast(F32), ALU.subtract
                                  ).then_inc(chunk_split, 1)

            low_e(0, 0, 0)
            dve.wait_ge(r_ps, NT)
            lg = comb[:, :, :]
            link(dve.tensor_tensor(lg, ps[4][:, 0:NT * N_EXP].rearrange("p (t e) -> p t e", t=NT),
                                   rb[:, :].unsqueeze(1).broadcast_to([P, NT, N_EXP]), ALU.add))
            dve.tensor_reduce(nmax[:, 0:NT], lg, AX.X, ALU.max, negate=True).then_inc(r_lg, 1)
            dve.wait_ge(r_exp, NT)
            link(dve.reciprocal(rsum[:, 0:NT], rsum[:, 0:NT]))
            link(dve.tensor_tensor(lg, lg, rsum[:, 0:NT].unsqueeze(2).broadcast_to([P, NT, N_EXP]), ALU.mult))
            pr = comb[:, :, :].rearrange("p t (g e) -> p (t g) e", g=GROUPS)

            def ranks(dst, v, n):
                mine = v.unsqueeze(3).broadcast_to([P, n, EPG, EPG])
                other = v.unsqueeze(2).broadcast_to([P, n, EPG, EPG])
                dve.tensor_tensor(r_gt[:, 0:n], other, mine, ALU.is_gt)
                link(dve.tensor_tensor(r_ge[:, 0:n], other, mine, ALU.is_ge))
                for i_ in range(1, EPG):
                    last = dve.tensor_copy(r_gt[:, 0:n, i_, 0:i_], r_ge[:, 0:n, i_, 0:i_])
                link(last)
                link(dve.tensor_reduce(dst, r_gt[:, 0:n], AX.X, ALU.add))

            ranks(r_top[:, :, :], pr, NG)
            link(dve.tensor_scalar(r_top[:, :, :], r_top[:, :, :], 1.5, None, ALU.is_lt))
            link(dve.tensor_tensor(r_pr[:, :, :], r_top[:, :, :], pr, ALU.mult))
            link(dve.tensor_reduce(r_gs[:, :, :].rearrange("p t g -> p (t g)"), r_pr[:, :, :], AX.X, ALU.add))
            ranks(r_best[:, :, :], r_gs[:, :, :], NT)
            best = r_best[:, :, :].rearrange("p t g -> p (t g)")
            link(dve.tensor_scalar(best, best, 0.5, None, ALU.is_lt))
            bestb = best.unsqueeze(2).broadcast_to([P, NG, EPG])
            dve.tensor_tensor(pr, r_top[:, :, :], bestb, ALU.mult).then_inc(r_sel, 1)
            link(dve.tensor_tensor(r_pr[:, :, :], r_pr[:, :, :], bestb, ALU.mult))
            link(dve.tensor_reduce(r_tot[:, :], r_pr[:, :, :].rearrange("p (t g) e -> p t (g e)", t=NT), AX.X, ALU.add))
            link(dve.reciprocal(r_tot[:, :], r_tot[:, :]))
            for cc in (1, 2):
                low_e(0, cc, 0)
            dve.wait_ge(pos_ps, 1)
            link(dve.scalar_tensor_tensor(out=posm[:, :, :].rearrange("p t e -> p (t e)"), in0=ps[5][:, 0:NT * N_EXP],
                                          scalar=1.0, in1=comb[:, :, :].rearrange("p t e -> p (t e)"),
                                          op0=ALU.add, op1=ALU.mult))
            link(dve.tensor_scalar(posm[:, :, :], posm[:, :, :], -1.0, None, ALU.add))
            link(dve.tensor_tensor(comb[:, :, :], r_pr[:, :, :].rearrange("p (t g) e -> p t (g e)", t=NT),
                                   r_tot[:, :].unsqueeze(2).broadcast_to([P, NT, N_EXP]), ALU.mult))
            link(dve.tensor_reduce(over_f[:, :], ps[6][:, 0:N_EXP], AX.X, ALU.max))
            dve.tensor_scalar(over[:, :], over_f[:, :], P + 0.5, None, ALU.is_gt).then_inc(route_ok, 1)

            def pick(X, e):
                if not isinstance(X, int) or X >= 2:
                    dve.wait_ge(selT_ps, X)
                for b in range(2):
                    dve.tensor_tensor(sel[:, :, b, :], iota[:, :].unsqueeze(1).broadcast_to([P, NT, P]),
                                      posm[:, :, bass.ds(e + b, 1)].broadcast_to([P, NT, P]), ALU.is_equal
                                      ).then_inc(sel_ready, 1)

            def y_low(X, b):
                for n in range(2):
                    dve.wait_ge(y_hi, 2 * X + n + 1)
                    dve.tensor_tensor(ye_lo[b][:, 512 * n:512 * n + 512], ps[5 + n][:, :],
                                      ye_hi[b][:, 512 * n:512 * n + 512].bitcast(F32), ALU.subtract).then_inc(y_sp, 1)

            def hg_low(X, u):
                dve.wait_ge(hg_hi, 2 * X + u + 1)
                part = lambda t: t[:, :, 2 * u:2 * u + 2, :].rearrange("p b k s -> p k b s")
                dve.tensor_tensor(part(hgT_lo), ps[2 + u % 2][:, :].rearrange("p (k b s) -> p k b s", k=2, b=2),
                                  part(hgT_hi).bitcast(F32), ALU.subtract).then_inc(hg_sp, 1)

            def adds(X, ks):
                for k in ks:
                    tt, n = k // 2, k % 2
                    dve.wait_ge(sc_ps, 4 * X + k + 1)
                    ya = yacc[:, tt, 512 * n:512 * n + 512]
                    dve.tensor_tensor(ya, ps[5 + k % 2][:, :], ya, ALU.add).then_inc(yadd, 1)

            def expert(X, e, b, first_, last_):
                if not first_:
                    y_low(X - 1, 1 - b)
                if b == 1 and not last_:
                    pick(X + 1, e + 1)
                spread = not first_ and b == 0
                low_e(X, 3, b)
                if spread:
                    adds(X - 2, (0, 1))
                low_e(X, 4, b)
                if spread:
                    adds(X - 2, (2, 3))
                low_e(X, 5, b)
                if spread:
                    adds(X - 2, (4, 5))
                dve.wait_ge(silu_ok, X + 1)
                dve.wait_ge(u_ps, X + 1)
                dve.wait_ge(ws_sb, X - b + 2)
                if not isinstance(X, int) or X >= 1:
                    dve.wait_ge(hidT_ps, X)
                dve.scalar_tensor_tensor(out=hid[:, :], in0=silu[:, :], scalar=slot_w[:, b:b + 1], in1=ps[1][:, :],
                                         op0=ALU.mult, op1=ALU.mult).then_inc(hid_ok, 1)
                if spread:
                    adds(X - 2, (6, 7))
                if b == 1 and not last_:
                    hg_low(X + 1, 0)
                    hg_low(X + 1, 1)
                dve.wait_ge(hidT_h, X + 1)
                dve.tensor_tensor(hidT_lo[:, :, :], ps[4][:, :].rearrange("p (k s) -> p k s", k=4),
                                  hidT_hi[:, :, :].bitcast(F32), ALU.subtract).then_inc(hidT_sp, 1)
                if not last_:
                    low_e(X + 1, 0, 1 - b)
                if b == 1 and not last_:
                    hg_low(X + 1, 2)
                if not last_:
                    low_e(X + 1, 1, 1 - b)
                if b == 1 and not last_:
                    hg_low(X + 1, 3)
                if not last_:
                    low_e(X + 1, 2, 1 - b)

            def expert_pass(X0):
                pick(X0, 0)
                if not isinstance(X0, int):
                    for cc in range(3):
                        low_e(X0, cc, 0)
                for u in range(4):
                    hg_low(X0, u)
                if isinstance(X0, int):
                    link(dve.memset(yacc[:, :, :], 0.0))
                expert(X0, 0, 0, True, False)
                expert(X0 + 1, 1, 1, False, False)
                with dve.Fori(1, N_EXP // 2 - 1) as q:
                    expert(X0 + q * 2, q * 2, 0, False, False)
                    expert(X0 + q * 2 + 1, q * 2 + 1, 1, False, False)
                expert(X0 + N_EXP - 2, N_EXP - 2, 0, False, False)
                expert(X0 + N_EXP - 1, N_EXP - 1, 1, False, True)
                y_low(X0 + N_EXP - 1, 1)
                adds(X0 + N_EXP - 2, range(8))

            expert_pass(0)
            dve.wait_ge(yadd, 4 * N_EXP)
            more = dve.value_load(over[0:1, 0:1], min_val=0, max_val=1)
            with dve.If(more > 0):
                with dve.Fori(1, PASSES) as p:
                    dve.wait_ge(selT_ps, p * N_EXP)
                    dve.tensor_scalar(posm[:, :, :], posm[:, :, :], float(-P), None, ALU.add).then_inc(posm_ok, 1)
                    dve.wait_ge(posm_ok, p)
                    expert_pass(p * N_EXP)
                    dve.wait_ge(yadd, (p + 1) * (4 * N_EXP))
                dve.nop()
            link(dve.memset(over_f[:, :], 0.0))
            dve.memset(over_f[:, :], 0.0).then_inc(moe_over, 1)
            dve.wait_ge(ld_g2, 16)
            for tt in range(NT):
                link(dve.tensor_tensor(yacc[:, tt, :], yacc[:, tt, :], gate2[:, :], ALU.mult))
                dve.tensor_tensor(xres[:, tt, :], xres[:, tt, :], yacc[:, tt, :], ALU.add).then_inc(out_sb, 1)


_INS = ["x", "c", "w_ada", "b_ada", "norm1_g", "w_in", "q_norm_g", "k_norm_g", "rel_bias", "w_o_a", "w_o_b", "w_out",
        "norm2_g", "router_w", "router_b", "w_gate", "w_up", "w_down"]


def kernel(**inputs):
    import concourse.bacc as bacc
    from concourse.bass_utils import run_bass_kernel_spmd

    nc = bacc.Bacc("TRN2", target_bir_lowering=False, num_devices=1)
    arrays = {f"in_{n}": np.ascontiguousarray(inputs[n]) for n in _INS}
    arrays["bucket_onehot"] = bucket_onehot()
    args = [nc.dram_tensor(n, a.shape, mybir.dt.from_np(a.dtype), kind="ExternalInput").ap() for n, a in arrays.items()]
    out = nc.dram_tensor("out", (1, S, D), F32, kind="ExternalOutput").ap()
    hybrid_layer(nc, *args, out)
    r = run_bass_kernel_spmd(nc, [arrays], core_ids=[0])
    return r.results[0]["out"]
```
